# Optimizing a Trainium2 kernel written in Bass

```python
import math
import jax, jax.numpy as jnp
from jax import lax
import numpy as np

D_MODEL = 1024
BATCH = 1
SEQ = 1024
DEPTH = 1

GRID_W = 64
CTX_LEN = 256
D_MIX = D_MODEL
HG_WIDTH = D_MIX // 2
HG_HEAD_DIM = 128
HG_HEADS = HG_WIDTH // HG_HEAD_DIM
HG_EXPAND = 128
HG_KDIM = HG_HEADS * HG_EXPAND
POOL_WIDTH = D_MIX - HG_WIDTH
POOL_WINDOWS = (2, 4, 8, 16)
POOL_GROUP = POOL_WIDTH // len(POOL_WINDOWS)
IN_COLS = 2 * HG_KDIM + HG_KDIM + 2 * HG_WIDTH + POOL_WIDTH
CHUNK = 64
N_EXPERTS = 32
TOP_K = 4
D_FF = D_MODEL
SWIGLU_LIMIT = 7.0
SWIGLU_ALPHA = 1.702
MOE_BLOCK = 128
EPS = 1e-6

kernel_name = "hybrid_hgrn2_pool_moe_dit_block"

def rms_norm(x, gain):
    xf = x.astype(jnp.float32)
    y = xf * lax.rsqrt(jnp.mean(xf * xf, axis=-1, keepdims=True) + EPS)
    return (y * gain.astype(jnp.float32)).astype(x.dtype)

def gla_chunked(q, k, v, logf, s0):
    B, H, T, DK = q.shape
    DV = v.shape[-1]
    n = T // CHUNK

    def to_chunks(a):
        return a.reshape(B, H, n, CHUNK, a.shape[-1]).transpose(2, 0, 1, 3, 4)

    causal = jnp.tril(jnp.ones((CHUNK, CHUNK), dtype=bool))[:, :, None]

    def step(S, inp):
        qc, kc, vc, lc = inp
        b = jnp.cumsum(lc, axis=-2)
        o_inter = jnp.einsum('bhtk,bhkv->bhtv', qc * jnp.exp(b), S)
        diff = b[:, :, :, None, :] - b[:, :, None, :, :]
        decay = jnp.exp(jnp.where(causal, diff, -jnp.inf))
        att = jnp.einsum('bhtk,bhsk,bhtsk->bhts', qc, kc, decay)
        o = o_inter + jnp.einsum('bhts,bhsv->bhtv', att, vc)
        b_last = b[:, :, -1:, :]
        S = jnp.exp(b_last[:, :, 0, :, None]) * S + jnp.einsum(
            'bhsk,bhsv->bhkv', kc * jnp.exp(b_last - b), vc)
        return S, o

    S, o = lax.scan(step, s0, (to_chunks(q), to_chunks(k), to_chunks(v), to_chunks(logf)))
    o = o.transpose(1, 2, 0, 3, 4).reshape(B, H, T, DV)
    return o, S

def hgrn2_mixer(p, lb, norm_gain, s0_f, s0_b):
    B, T, _ = p.shape
    q, ff, fb, i, g = jnp.split(p, [HG_KDIM, 2 * HG_KDIM, 3 * HG_KDIM, 3 * HG_KDIM + HG_WIDTH], axis=-1)

    def heads(a):
        return a.reshape(B, T, HG_HEADS, -1).transpose(0, 2, 1, 3).astype(jnp.float32)

    qh = heads(jax.nn.silu(q))
    vh = heads(i)

    def direction(fpre, lbd, s0, reverse):
        fz = heads(fpre)
        lbh = lbd.astype(jnp.float32).reshape(HG_HEADS, 1, HG_EXPAND)
        logf = jnp.log(lbh + (1.0 - lbh) * jax.nn.sigmoid(fz))
        kk = (1.0 - lbh) * jax.nn.sigmoid(-fz)
        qq, vv = qh, vh
        if reverse:
            qq, kk, vv, logf = (jnp.flip(a, axis=2) for a in (qq, kk, vv, logf))
        o, s = gla_chunked(qq, kk, vv, logf, s0)
        if reverse:
            o = jnp.flip(o, axis=2)
        return o, s

    o_f, s_f = direction(ff, lb[0], s0_f, False)
    o_b, s_b = direction(fb, lb[1], s0_b, True)
    o = o_f + o_b
    o = o * lax.rsqrt(jnp.mean(o * o, axis=-1, keepdims=True) + EPS)
    o = o.transpose(0, 2, 1, 3).reshape(B, T, HG_WIDTH)
    o = o * norm_gain.astype(jnp.float32) * jax.nn.sigmoid(g.astype(jnp.float32))
    return o.astype(p.dtype), s_f, s_b

def window_mean(x, axis, w):
    n = x.shape[axis]
    cs = jnp.cumsum(x.astype(jnp.float32), axis=axis)
    zero = jnp.zeros_like(lax.slice_in_dim(cs, 0, 1, axis=axis))
    cs = jnp.concatenate([zero, cs], axis=axis)
    t = jnp.arange(n)
    lo = jnp.clip(t - w // 2, 0, n)
    hi = jnp.clip(t - w // 2 + w, 0, n)
    s = jnp.take(cs, hi, axis=axis) - jnp.take(cs, lo, axis=axis)
    shape = [1] * x.ndim
    shape[axis] = n
    cnt = (hi - lo).astype(jnp.float32).reshape(shape)
    return s / cnt

def pool_mixer(u, pool_w, pool_scale, rows):
    B, T, _ = u.shape
    outs = []
    for gi, w in enumerate(POOL_WINDOWS):
        ug = u[..., gi * POOL_GROUP:(gi + 1) * POOL_GROUP].astype(jnp.float32)
        if rows is None:
            m = window_mean(ug, 1, w)
        else:
            grid = ug.reshape(B, rows, GRID_W, POOL_GROUP)
            m = window_mean(window_mean(grid, 1, w), 2, w).reshape(B, T, POOL_GROUP)
        outs.append(jnp.einsum('btc,cd->btd', m - ug, pool_w[gi].astype(jnp.float32)))
    y = jnp.concatenate(outs, axis=-1) * pool_scale.astype(jnp.float32)
    return y.astype(u.dtype)

def moe(xt, w_router, b_router, w_gate, b_gate, w_up, b_up, w_down, b_down):
    T, D = xt.shape
    logits = (xt @ w_router + b_router).astype(jnp.float32)
    top_val, top_idx = lax.top_k(logits, TOP_K)
    top_w = jax.nn.softmax(top_val, axis=-1)
    A = T * TOP_K
    flat_e = top_idx.reshape(-1).astype(jnp.int32)
    flat_tok = jnp.arange(A, dtype=jnp.int32) // TOP_K
    flat_w = top_w.reshape(-1)
    order = jnp.argsort(flat_e, stable=True)
    sorted_e = flat_e[order]
    counts = jnp.bincount(flat_e, length=N_EXPERTS)
    padded = ((counts + MOE_BLOCK - 1) // MOE_BLOCK) * MOE_BLOCK
    start = jnp.cumsum(counts) - counts
    pend = jnp.cumsum(padded)
    pstart = pend - padded
    rank = jnp.arange(A, dtype=jnp.int32) - start[sorted_e]
    dest = pstart[sorted_e] + rank
    n_blocks = -(-A // MOE_BLOCK) + N_EXPERTS
    P = n_blocks * MOE_BLOCK
    row_tok = jnp.full((P,), T, dtype=jnp.int32).at[dest].set(flat_tok[order])
    row_w = jnp.zeros((P,), jnp.float32).at[dest].set(flat_w[order])
    block_e = jnp.clip(jnp.searchsorted(pend, jnp.arange(n_blocks) * MOE_BLOCK, side='right'), 0, N_EXPERTS - 1)
    xpad = jnp.concatenate([xt, jnp.zeros((1, D), xt.dtype)], axis=0)
    xb = xpad[row_tok].reshape(n_blocks, MOE_BLOCK, D)

    def expert_block(args):
        xblk, e = args
        gate = xblk @ w_gate[e] + b_gate[e]
        up = xblk @ w_up[e] + b_up[e]
        gate = jnp.minimum(gate, SWIGLU_LIMIT)
        up = jnp.clip(up, -SWIGLU_LIMIT, SWIGLU_LIMIT)
        h = (up + 1.0) * gate * jax.nn.sigmoid(SWIGLU_ALPHA * gate)
        return h @ w_down[e] + b_down[e]

    yb = lax.map(expert_block, (xb, block_e)).reshape(P, D)
    y = jax.ops.segment_sum(yb.astype(jnp.float32) * row_w[:, None], row_tok, num_segments=T + 1)[:T]
    return y.astype(xt.dtype)

def setup_inputs(seed: int = 0) -> dict:
    key = jax.random.key(seed)
    ks = jax.random.split(key, 26)
    L, D, E, F = DEPTH, D_MODEL, N_EXPERTS, D_FF
    nrm = lambda k, s, sc: jax.random.normal(k, s, jnp.float32) * sc
    return {
        "x": nrm(ks[0], (BATCH, SEQ, D), 1.0),
        "c": nrm(ks[1], (BATCH, D), 1.0),
        "ctx": nrm(ks[2], (BATCH, CTX_LEN, D), 1.0),
        "c_ctx": nrm(ks[3], (D,), 1.0),
        "w_ada": nrm(ks[4], (L, D, 6 * D), 0.5 / math.sqrt(D)),
        "b_ada": nrm(ks[5], (L, 6 * D), 0.02),
        "g_pre_mix": 1.0 + nrm(ks[6], (L, D), 0.02),
        "g_post_mix": 1.0 + nrm(ks[7], (L, D), 0.02),
        "g_pre_ffn": 1.0 + nrm(ks[8], (L, D), 0.02),
        "g_post_ffn": 1.0 + nrm(ks[9], (L, D), 0.02),
        "w_in": nrm(ks[10], (L, D, IN_COLS), 1.0 / math.sqrt(D)),
        "w_out": nrm(ks[11], (L, D_MIX, D), 1.0 / math.sqrt(D_MIX)),
        "hgrn_lb_logits": nrm(ks[12], (L + 1, 2, HG_KDIM), 0.1),
        "hgrn_norm": 1.0 + nrm(ks[13], (L, HG_WIDTH), 0.02),
        "pool_w": nrm(ks[14], (L, len(POOL_WINDOWS), POOL_GROUP, POOL_GROUP), 1.0 / math.sqrt(POOL_GROUP)),
        "pool_scale": 1.0 + nrm(ks[15], (L, POOL_WIDTH), 0.1),
        "w_router": nrm(ks[16], (L, D, E), 1.0 / math.sqrt(D)),
        "b_router": nrm(ks[17], (L, E), 0.01),
        "w_gate": nrm(ks[18], (L, E, D, F), 1.0 / math.sqrt(D)),
        "b_gate": nrm(ks[19], (L, E, F), 0.01),
        "w_up": nrm(ks[20], (L, E, D, F), 1.0 / math.sqrt(D)),
        "b_up": nrm(ks[21], (L, E, F), 0.01),
        "w_down": nrm(ks[22], (L, E, F, D), 1.0 / math.sqrt(F)),
        "b_down": nrm(ks[23], (L, E, D), 0.01),
    }

def reference(x, c, ctx, c_ctx, w_ada, b_ada, g_pre_mix, g_post_mix, g_pre_ffn, g_post_ffn,
              w_in, w_out, hgrn_lb_logits, hgrn_norm, pool_w, pool_scale,
              w_router, b_router, w_gate, b_gate, w_up, b_up, w_down, b_down):
    B, S, D = x.shape
    rows = S // GRID_W
    Bc, Tc, _ = ctx.shape
    lb_table = jnp.cumsum(jax.nn.softmax(hgrn_lb_logits.astype(jnp.float32), axis=0), axis=0)

    for l in range(DEPTH):
        last = l == DEPTH - 1
        mod_lat = (jax.nn.silu(c) @ w_ada[l] + b_ada[l])[:, None, :]
        mod_ctx = (jax.nn.silu(c_ctx) @ w_ada[l] + b_ada[l])[None, None, :]
        sh1, sc1, gt1, sh2, sc2, gt2 = jnp.split(mod_lat, 6, axis=-1)
        csh1, csc1, cgt1, csh2, csc2, cgt2 = jnp.split(mod_ctx, 6, axis=-1)
        lb = lb_table[l]

        hc = rms_norm(ctx, g_pre_mix[l]) * (1.0 + csc1) + csh1
        pc = hc @ w_in[l]
        zeros_state = jnp.zeros((Bc, HG_HEADS, HG_EXPAND, HG_HEAD_DIM), jnp.float32)
        o_hg_c, s_f, s_b = hgrn2_mixer(pc[..., :IN_COLS - POOL_WIDTH], lb, hgrn_norm[l], zeros_state, zeros_state)

        hx = rms_norm(x, g_pre_mix[l]) * (1.0 + sc1) + sh1
        px = hx @ w_in[l]
        o_hg_x, _, _ = hgrn2_mixer(px[..., :IN_COLS - POOL_WIDTH], lb, hgrn_norm[l], s_f, s_b)
        o_pool_x = pool_mixer(px[..., IN_COLS - POOL_WIDTH:], pool_w[l], pool_scale[l], rows)
        yx = jnp.concatenate([o_hg_x, o_pool_x], axis=-1) @ w_out[l]
        x = x + gt1 * rms_norm(yx, g_post_mix[l])

        if not last:
            o_pool_c = pool_mixer(pc[..., IN_COLS - POOL_WIDTH:], pool_w[l], pool_scale[l], None)
            yc = jnp.concatenate([o_hg_c, o_pool_c], axis=-1) @ w_out[l]
            ctx = ctx + cgt1 * rms_norm(yc, g_post_mix[l])

        hx2 = (rms_norm(x, g_pre_ffn[l]) * (1.0 + sc2) + sh2).reshape(B * S, D)
        if last:
            tokens = hx2
        else:
            hc2 = (rms_norm(ctx, g_pre_ffn[l]) * (1.0 + csc2) + csh2).reshape(Bc * Tc, D)
            tokens = jnp.concatenate([hx2, hc2], axis=0)
        y = moe(tokens, w_router[l], b_router[l], w_gate[l], b_gate[l], w_up[l], b_up[l], w_down[l], b_down[l])
        x = x + gt2 * rms_norm(y[:B * S].reshape(B, S, D), g_post_ffn[l])
        if not last:
            ctx = ctx + cgt2 * rms_norm(y[B * S:].reshape(Bc, Tc, D), g_post_ffn[l])

    return x


_drawn_inputs = setup_inputs


def setup_inputs(seed=0):
    import zlib

    import numpy as np

    out = dict(_drawn_inputs(seed))
    spreads = {}
    factors = {'ctx': 6.955,
     'c_ctx': 8.0,
     'g_pre_mix': 3.838,
     'g_post_mix': 3.349,
     'g_post_ffn': 8.0,
     'hgrn_lb_logits': 8.0,
     'hgrn_norm': 5.713,
     'b_router': 3.001,
     'b_gate': 8.0,
     'b_up': 8.0,
     'b_down': 8.0}
    for name, (base, spread) in spreads.items():
        noise = np.random.default_rng([zlib.crc32(name.encode()), seed]).standard_normal(out[name].shape)
        drawn = base * np.exp(spread * noise) if base else spread * noise
        out[name] = __import__('jax').numpy.asarray(drawn.astype(out[name].dtype))
    for name, factor in factors.items():
        out[name] = (out[name] * factor).astype(out[name].dtype)
    return out
```

```python
from contextlib import ExitStack

import concourse.bass as bass
from concourse import mybir

ALU = mybir.AluOpType
ACT = mybir.ActivationFunctionType
AX_X = mybir.AxisListType.X
F32 = mybir.dt.float32
BF16 = mybir.dt.bfloat16
U32 = mybir.dt.uint32
I32 = mybir.dt.int32

P = 128
KIB = 1024
EPS = 1e-6
SWIGLU_LIMIT = 7.0
SWIGLU_ALPHA = 1.702
TOP_K = 4
GRID_W = 64
WINDOWS = (2, 4, 8, 16)
PAD = max(WINDOWS) // 2
LEVELS = 7
BLOCK = 256
STEP = 64
FAR = 8192.0


def hybrid_block_kernel(nc, x, c, ctx_tok, c_ctx, w_ada, b_ada, g_pre_mix, g_post_mix, g_pre_ffn,
                        g_post_ffn, w_in, w_out, lb_logits, hgrn_norm, pool_w, pool_scale, w_router,
                        b_router, w_gate, b_gate, w_up, b_up, w_down, b_down, out):
    SEQ, D = x.shape[1], x.shape[2]
    CTX = ctx_tok.shape[1]
    KT = D // P
    TL, TC = SEQ // P, CTX // P
    NT, TOK = TL + TC, SEQ + CTX
    HG = hgrn_norm.shape[1]
    HEADS = HG // P
    NE = w_router.shape[2]
    GRID_H = SEQ // GRID_W
    NG = len(WINDOWS)
    HALF = D // 2
    OVER = TOP_K * SEQ // BLOCK
    CHUNKS = SEQ // BLOCK - 1
    NTAB = NE + OVER + 4
    VARIANTS = range(1, BLOCK // STEP + 1)
    QW = 256
    NQ = D // QW

    with ExitStack() as st:
        def sem(name):
            return st.enter_context(nc.semaphore(name))

        def region(lo, hi):
            at = [16512 + int(lo * KIB)]

            def take(name, *shape, dt=F32, parts=P):
                n = 2 if dt == BF16 else 4
                for s in shape:
                    n *= s
                t = nc.alloc_sbuf_tensor_at(name, [parts, *shape], dt, offset=at[0])
                at[0] += (n + 31) // 32 * 32
                assert at[0] <= 16512 + hi * KIB, name
                return t

            return take

        ps = st.enter_context(nc.psum_tensor("ps", [P, 8, 512], F32))
        xn_dram = nc.dram_tensor("xn_rows", [SEQ, D], F32).ap()
        y_dram = nc.dram_tensor("y_rows", [SEQ + BLOCK, D], F32).ap()

        hxT = region(0, 40)("hxT", KT, TOK)
        r = region(40, 64)
        ring = [r(f"w_ring{s}", KT, QW) for s in range(3)]
        r = region(64, 108)
        x_all, junk = r("x_all", NT, D), r("junk", D)
        r = region(64, 133)
        Qd = [r("q_fwd", SEQ), r("q_bwd", SEQ)]
        Kd = [r("k_fwd", TOK), r("k_bwd", TOK)]
        Fd = [r("f_fwd", TOK), r("f_bwd", TOK)]
        q_s = r("q_sig", SEQ)
        sig_f, sig_k = [None, None], [None, None]
        for d in range(2):
            sig_f[d], sig_k[d] = r(f"sig_f{d}", TOK), r(f"sig_nf{d}", TOK)
        kT_sb = [r("kT0", 512), r("kT1", 512)]
        states = [r("s_fwd", TL + 1, P), r("s_bwd", TL + 1, P)]
        att = [None, r("att1", TL, P)]
        r = region(133, 193)
        att[0], q_raw = r("att0", TL, P), r("q_raw", SEQ)
        v_tok, sig_g, o_tok = r("v_tok", NT, HG), r("sig_g", TL, HG), r("o_tok", TL, HG)
        r = region(92, 116)
        u_T, box0 = r("u_T", NG, SEQ), r("box0", 2048)
        box = [box0, region(133, 141)("box1", 2048)]
        vec_rows = region(161, 162)("vec_rows", P, parts=120)
        mixT = region(0, 32)("mixT", 2 * HEADS, SEQ)
        r = region(40, 72)
        wo_sb = [r(f"w_out{s}", KT, QW) for s in range(D // QW)]
        x1 = region(108, 140)("x1", TL, D)
        r = region(141, 165)
        hx2T = [r("hx2T0", KT, P), r("hx2T1", KT, P)]
        xn_t = [r("xn0", D), r("xn1", D)]
        gain = [None, r("gain_ffn", D)]
        gain[0] = r("gain_mix", D)
        bias_rows = region(165, 177)("bias_rows", 3, D, parts=NE)
        r = region(165, 177)
        cand_oh, cand_v = r("cand_oh", OVER, NE * CHUNKS), r("cand_v", OVER, NE * CHUNKS)
        wide_t = region(177, 181)("wide_t", D)
        r = region(96, 104)
        logit, mask, onehot, wtmp = (r(n, TL, NE) for n in ("logit", "mask", "onehot", "wtmp"))
        mask_bf = r("mask_bf", TL, NE, dt=BF16)
        w_route, top_v, top_f = r("w_route", TL, TOP_K), r("top_v", TL, 8), r("top_f", TL, 8)
        top_i = r("top_i", TL, 8, dt=U32)
        row_t = r("row_t", 3, TL)
        cnt, tab_c, tab_v = r("cnt", NE), r("tab_c", NTAB), r("tab_v", NTAB)
        cand_has, cand_rank, cand_e, cand_b, cand_c = (
            r(n, NE * CHUNKS) for n in ("cand_has", "cand_rank", "cand_e", "cand_b", "cand_c"))
        r = region(0, 96)
        wgt = [r(n, KT, D) for n in ("w_gate_e", "w_up_e", "w_down_e")]
        sel = region(96, 104)("sel", TL, BLOCK)
        r = region(104, 108)
        biasT, gate0 = r("biasT", 3 * KT, NE), r("gate0", BLOCK)
        gate_sb = [gate0, region(140, 141)("gate1", BLOCK)]
        r = region(141, 157)
        xg, xT = r("xg", 2, D), r("xT", KT, BLOCK)
        r = region(161, 189)
        up_sb, sig_sb = [r("up0", BLOCK), r("up1", BLOCK)], [r("sig0", BLOCK), r("sig1", BLOCK)]
        hT, yT, yrow = r("hT", KT, BLOCK), r("yT", KT, BLOCK), r("yrow", 2, D)
        r = region(189, 193)
        pos, rtab = r("pos", TL, NE), r("rtab", TL, NE + 2)
        iota_b, cnt_t = r("iota_b", BLOCK), r("cnt_t", GRID_W)
        r = region(193, 206.84375)
        ident, ones, vecT = r("ident", P), r("ones", P), r("vecT", 120)
        cT, sigc = r("cT", KT, 2), r("sigc", 2, KT)
        lbd, lbT = r("lbd", 2 * HEADS), r("lbT", 2, 2 * HEADS)
        mod, A1, A2, gpost = r("mod", 6 * KT, 2), r("A1", KT, 2), r("A2", KT), r("gpost", 2, KT)
        ssq, rs_v, rs_s, rs_t, rstd = (r(n, 40) for n in ("ssq", "rs_v", "rs_s", "rs_t", "rstd"))
        wr_sb, br_sb, pw_sb = r("wr_sb", KT, NE), r("br_sb", NE, parts=1), r("pw_sb", NG, P)
        masks = r("masks", 2, LEVELS, P // 2)
        cnt_c, cnt_r = r("cnt_c", NG, GRID_W), r("cnt_r", NG, GRID_H)
        iota_e, upper_bf, ones_bf = r("iota_e", NE), r("upper_bf", P, dt=BF16), r("ones_bf", P, dt=BF16)
        upper_f = r("upper_f", P)
        tab_e, tab_b = r("tab_e", NTAB), r("tab_b", NTAB)
        int_e, int_v, int_h, int_n = (r(n, w, dt=I32) for n, w in (("int_e", NTAB), ("int_v", NTAB), ("int_h", NTAB),
                                                                   ("int_n", 8)))
        n_items_f = r("n_items_f", 8)
        posc, bias_gu, bias_d = r("posc", TL), r("bias_gu", 2 * KT), r("bias_d", KT)
        w_next, w_cur, sidx_f = r("w_next", 2), r("w_cur", 2), r("sidx_f", 2)
        gidx, sidx, sidx_cur = (r(n, 2, dt=U32) for n in ("gidx", "sidx", "sidx_cur"))
        spare = r("spare", 2)
        r = region(206.84375, 207.875)
        diag_t, o_junk = r("diag_t", P), r("o_junk", P)
        slot_ids = region(206.84375, 207.875)("slot_ids", BLOCK)

        V_BADA, V_GPM, V_GQM, V_GPF, V_GQF, V_C, V_CC = 0, 48, 56, 64, 72, 80, 88
        V_NORM, V_SCALE, V_LB = 96, 100, 104

        chunks, units = [], []

        def chunk(parts, new_units):
            for u in new_units:
                units.append((*u, len(chunks)))
            chunks.append((parts, len(units)))

        for n in (*range(KT // 2, KT), *range(KT // 2)):
            chunk([(w_ada, n * QW, QW)], [("a", 2 * n), ("a", 2 * n + 1)])
        n_ada_first = len(units)
        for h2 in range(2):
            chunk([(w_in, 3 * HG + h2 * QW, QW)], [("v", t, h2) for t in range(NT)])
        window = [len(units)]
        for h in range(HEADS):
            chunk([(w_in, HG + h * P, P), (w_in, 2 * HG + h * P, P)],
                  [("f", h, d, part) for d in range(2) for part in range(3)])
            chunk([(w_in, h * P, P)], [("q", h, 0, part) for part in range(2)])
            window.append(len(units))
        for g2 in range(2):
            chunk([(w_in, 5 * HG + g2 * QW, QW)], [("u", 2 * g2 + k, part) for k in range(2) for part in range(2)])
        n_units_u = len(units)
        for h2 in range(2):
            chunk([(w_in, 4 * HG + h2 * QW, QW)], [("g", t, h2) for t in range(TL)])
        for n in range(KT, 3 * KT):
            chunk([(w_ada, n * QW, QW)], [("a", 2 * n), ("a", 2 * n + 1)])
        window.append(len(units))
        evac_before = [0]
        for u in units:
            evac_before.append(evac_before[-1] + (u[0] != "a"))
        SLOTS = LEVELS + 6
        head_units = []
        for h in range(HEADS):
            lo, hi = window[h + 1], window[h + 2]
            cut = [lo + (hi - lo) * s // SLOTS for s in range(SLOTS + 1)]
            head_units.append([range(cut[s], cut[s + 1]) for s in range(SLOTS)])

        SCAN = [[TL, TL + 1, *range(TL - 1)], [TL + 1, TL, *range(TL - 1, 0, -1)]]
        BATCHES = [(d, lo, min(lo + 4, TL + 1)) for d in range(2) for lo in range(0, TL + 1, 4)]

        def state_slot(n):
            return TL if n == 0 else n - 1

        XGROUPS = [(k, t0, nt, s) for k in range(KT) for t0, nt, s in ((0, 4, 0), (4, 4, 0), (TL, TC, 1))]

        vec_in, x_in, ctx_in, misc_in = sem("vec_in"), sem("x_in"), sem("ctx_in"), sem("misc_in")
        ring_in = [sem(f"ring_in{s}") for s in range(3)]
        consts, passed = sem("consts"), sem("passed")
        pool_chain, dve_chain, act_chain = sem("pool_chain"), sem("dve_chain"), sem("act_chain")
        vec_psum, vec_sb, cond_sig, cond_ready, lb_ready = (
            sem(n) for n in ("vec_psum", "vec_sb", "cond_sig", "cond_ready", "lb_ready"))
        lb_diff = sem("lb_diff")
        ada_psum, mod_ready = sem("ada_psum"), sem("mod_ready")
        sq_done, var_ready, root_ready = sem("sq_done"), sem("var_ready"), sem("root_ready")
        xn_ready = sem("xn_ready")
        xt0_psum, xt0_act, xt0_dve = sem("xt0_psum"), sem("xt0_act"), sem("xt0_dve")
        proj_psum, proj_evac = sem("proj_psum"), sem("proj_evac")
        qk_ready, lev_psum, lev_put = sem("qk_ready"), sem("lev_psum"), sem("lev_put")
        diag_psum, diag_put = sem("diag_psum"), sem("diag_put")
        kT_psum, kT_ready, u_psum, state_ready = sem("kT_psum"), sem("kT_ready"), sem("u_psum"), sem("state_ready")
        o_psum, o_ready = sem("o_psum"), sem("o_ready")
        box_used = sem("box_used")
        gated, oT_psum, mix_ready = sem("gated"), sem("oT_psum"), sem("mix_ready")
        wo_in, x1_in, brow_in = sem("wo_in"), sem("x1_in"), sem("brow_in")
        diag_ready, diag_used, gain_ready = (sem(n) for n in ("diag_ready", "diag_used", "gain_ready"))
        yx_psum, yx_used, xn2_ready, xt2_psum, xt2_ready = (
            sem(n) for n in ("yx_psum", "yx_used", "xn2_ready", "xt2_psum", "xt2_ready"))
        xn2_out, y_in = [[sem(f"{n}{k}") for k in range(2)] for n in ("xn2_out", "y_in")]
        logit_psum, bt_psum, bt_ready = sem("logit_psum"), sem("bt_psum"), sem("bt_ready")
        top_diff, top_exp, mask_ready, pos_psum, tables = (
            sem(n) for n in ("top_diff", "top_exp", "mask_ready", "pos_psum", "tables"))
        zero_ready = sem("zero_ready")
        w_exp = [[sem(f"{m}_in{q}") for q in range(NQ)] for m in ("gate", "up", "down")]
        sel_ready, sel_psum, idx_ready = sem("sel_ready"), sem("sel_psum"), sem("idx_ready")
        ids_ready = sem("ids_ready")
        xg_in = [sem("xg_in0"), sem("xg_in1")]
        xT_psum, xT_ready = sem("xT_psum"), sem("xT_ready")
        gu_psum, gate_ready, gu_evac, sig_ready, h_ready = (
            sem(n) for n in ("gu_psum", "gate_ready", "gu_evac", "sig_ready", "h_ready"))
        d_psum, yT_ready, yr_psum, yr_ready = sem("d_psum"), sem("yT_ready"), sem("yr_psum"), sem("yr_ready")
        w_copied, sidx_copied = sem("w_copied"), sem("sidx_copied")
        y_added = [sem("y_added0"), sem("y_added1")]
        fin_sq, fin_ready, out_done = (sem(n) for n in ("fin_sq", "fin_ready", "out_done"))

        Y_ZERO = (SEQ + BLOCK) // (2 * P)

        def loop_count(eng):
            return eng.value_load(int_n[0:1, 0:1], min_val=NE, max_val=NE + OVER)

        def item_expert(eng, i):
            return eng.value_load(int_e[0:1, bass.ds(i, 1)], min_val=0, max_val=NE - 1)

        def item_variant(eng, i):
            return eng.value_load(int_v[0:1, bass.ds(i, 1)], min_val=1, max_val=len(VARIANTS))

        def large_before(eng, i):
            return eng.value_load(int_h[0:1, bass.ds(i, 1)], min_val=0, max_val=NE + OVER)

        def apart(eng):
            eng.sem_inc(passed, 1)

        def cols(w):
            return w[0].rearrange("(k p) n -> p k n", p=P)

        def chunk_is_used(eng, n):
            last = chunks[n][1] - 1
            if units[last][0] == "a":
                eng.wait_ge(ada_psum, last + 1 - evac_before[last])
            else:
                eng.wait_ge(proj_psum, evac_before[last + 1])

        block = st.enter_context(nc.Block())

        @block.sync
        def _(sp):
            for row, n, src in ((V_BADA, 48, b_ada), (V_GPM, KT, g_pre_mix), (V_GQM, KT, g_post_mix),
                                (V_GPF, KT, g_pre_ffn), (V_GQF, KT, g_post_ffn), (V_C, KT, c),
                                (V_CC, KT, c_ctx), (V_NORM, HEADS, hgrn_norm), (V_SCALE, NG, pool_scale)):
                flat = src if len(src.shape) == 1 else src[0]
                sp.dma_start(vec_rows[row:row + n, :], flat.rearrange("(a b) -> a b", b=P)).then_inc(vec_in, 16)
            sp.dma_start(vec_rows[V_LB:V_LB + 4 * HEADS, :],
                         lb_logits.rearrange("l d (h k) -> (l d h) k", k=P)).then_inc(vec_in, 16)
            sp.dma_start(x_all[:, 0:TL, :], x[0].rearrange("(t p) d -> p t d", p=P)).then_inc(x_in, 16)
            sp.dma_start(x_all[:, TL:NT, :], ctx_tok[0].rearrange("(t p) d -> p t d", p=P)).then_inc(ctx_in, 16)
            sp.dma_start(pw_sb[:], pool_w[0].rearrange("g c d -> c g d")).then_inc(misc_in, 16)
            sp.dma_start(wr_sb[:], w_router[0].rearrange("(k p) e -> p k e", p=P)).then_inc(misc_in, 16)
            sp.dma_start(br_sb[:], b_router).then_inc(misc_in, 16)
            for n, (parts, _) in enumerate(chunks):
                if n >= 3:
                    chunk_is_used(sp, n - 3)
                at = 0
                for w, col, width in parts:
                    sp.dma_start(ring[n % 3][:, :, at:at + width],
                                 cols(w)[:, :, col:col + width]).then_inc(ring_in[n % 3], 16)
                    at += width
            for n in range(len(chunks) - 3, len(chunks)):
                chunk_is_used(sp, n)
            for q in range(3):
                sp.dma_start(wo_sb[q][:], cols(w_out)[:, :, q * QW:(q + 1) * QW]).then_inc(wo_in, 16)
            sp.wait_ge(o_psum, 2 * HEADS)
            sp.dma_start(wo_sb[3][:], cols(w_out)[:, :, 3 * QW:4 * QW]).then_inc(wo_in, 16)
            sp.wait_ge(box_used, NG)
            sp.dma_start(x1[:], x[0].rearrange("(t p) d -> p t d", p=P)).then_inc(x1_in, 16)
            sp.wait_ge(oT_psum, HEADS * 2)
            for m, b in enumerate((b_gate, b_up, b_down)):
                sp.dma_start(bias_rows[:, m, :], b[0]).then_inc(brow_in, 16)
            for t in range(TL):
                sp.wait_ge(xn2_ready, t + 1)
                sp.dma_start(xn_dram[t * P:(t + 1) * P, :], xn_t[t % 2][:]).then_inc(xn2_out[t % 2], 16)
            sp.wait_ge(yx_psum, TL)
            exps = [w[0].rearrange("e (k p) n -> e p k n", p=P) for w in (w_gate, w_up, w_down)]
            for q in range(NQ):
                for m in (0, 1):
                    sp.dma_start(wgt[m][:, :, q * QW:(q + 1) * QW],
                                 exps[m][0, :, :, q * QW:(q + 1) * QW]).then_inc(w_exp[m][q], 16)
            for q in range(NQ):
                sp.dma_start(wgt[2][:, :, q * QW:(q + 1) * QW],
                             exps[2][0, :, :, q * QW:(q + 1) * QW]).then_inc(w_exp[2][q], 16)
            sp.wait_ge(tables, 1)
            n_items = loop_count(sp)
            with sp.Fori(0, n_items - 1) as i:
                e = item_expert(sp, i + 1)
                for q in range(NQ):
                    sp.wait_ge(gu_psum, i * KT + 2 * (q + 1))
                    for m in (0, 1):
                        sp.dma_start(wgt[m][:, :, q * QW:(q + 1) * QW],
                                     exps[m][bass.ds(e, 1), :, :, q * QW:(q + 1) * QW].rearrange(
                                         "o p k n -> p (o k) n")).then_inc(w_exp[m][q], 16)
                for q in range(NQ):
                    sp.wait_ge(d_psum, i * KT + 2 * (q + 1))
                    sp.dma_start(wgt[2][:, :, q * QW:(q + 1) * QW],
                                 exps[2][bass.ds(e, 1), :, :, q * QW:(q + 1) * QW].rearrange(
                                     "o p k n -> p (o k) n")).then_inc(w_exp[2][q], 16)
            sp.wait_ge(y_added[0], n_items * 16 + 16 * Y_ZERO)
            sp.wait_ge(y_added[1], large_before(sp, n_items) * 16 + 16 * Y_ZERO)
            for t in range(TL):
                if t >= 2:
                    sp.wait_ge(fin_ready, t - 1)
                sp.dma_start(xn_t[t % 2][:], y_dram[t * P:(t + 1) * P, :]).then_inc(y_in[t % 2], 16)
                if t >= 1:
                    sp.wait_ge(fin_ready, t)
                    sp.dma_start(out[0, (t - 1) * P:t * P, :], x1[:, t - 1, :]).then_inc(out_done, 16)
            sp.wait_ge(fin_ready, TL)
            sp.dma_start(out[0, (TL - 1) * P:SEQ, :], x1[:, TL - 1, :]).then_inc(out_done, 16)
            sp.wait_ge(out_done, 16 * TL)

        @block.gpsimd
        def _(pool):
            count = [0]

            def link(ins):
                count[0] += 1
                ins.then_inc(pool_chain, 1)
                pool.wait_ge(pool_chain, count[0])

            G = nc.gpsimd
            link(G.memset(ident[:], 0.0))
            G.affine_select(out=ident[:], in_=ident[:], compare_op=ALU.not_equal, fill=1.0, base=0,
                            pattern=[[-1, P]], channel_multiplier=1).then_inc(consts, 1)
            link(G.memset(ones[:], 1.0))
            link(G.memset(masks[:], 1.0))
            for lv in range(LEVELS):
                h = 1 << lv
                nb = P // (2 * h)
                for d in range(2):
                    m = masks[:, d, lv, :].rearrange("p (b j) -> p b j", b=nb)
                    lo = h * d
                    link(G.affine_select(out=m, in_=m, compare_op=ALU.is_ge, fill=0.0, base=-lo,
                                         pattern=[[-2 * h, nb], [0, h]], channel_multiplier=1))
                    link(G.affine_select(out=m, in_=m, compare_op=ALU.is_ge, fill=0.0, base=lo + h - 1,
                                         pattern=[[2 * h, nb], [0, h]], channel_multiplier=-1))
            link(G.memset(upper_f[:], 1.0))
            link(G.affine_select(out=upper_f[:], in_=upper_f[:], compare_op=ALU.is_gt, fill=0.0, base=0,
                                 pattern=[[1, P]], channel_multiplier=-1))
            G.tensor_copy(upper_bf[:], upper_f[:])
            link(G.tensor_copy(ones_bf[:], ones[:]))
            for n, tabl in ((GRID_W, cnt_c), (GRID_H, cnt_r)):
                link(G.iota(cnt_t[:, 0:n], pattern=[[1, n]], base=0, channel_multiplier=0,
                            allow_small_or_imprecise_dtypes=True))
                for g, w in enumerate(WINDOWS):
                    link(G.tensor_scalar(tabl[:, g, :], cnt_t[:, 0:n], float(w // 2), float(n), ALU.add, ALU.min))
                    link(G.tensor_scalar(iota_b[:, 0:n], cnt_t[:, 0:n], float(-(w // 2)), 0.0, ALU.add, ALU.max))
                    link(G.tensor_tensor(tabl[:, g, :], tabl[:, g, :], iota_b[:, 0:n], ALU.subtract))
            G.iota(iota_e[:], pattern=[[1, NE]], base=0, channel_multiplier=0, allow_small_or_imprecise_dtypes=True)
            G.iota(spare[:], pattern=[[P, 2]], base=SEQ, channel_multiplier=1, allow_small_or_imprecise_dtypes=True)
            link(G.memset(tab_e[:], 0.0))
            G.memset(tab_b[:], 0.0).then_inc(consts, 1)

            pool.wait_ge(proj_evac, evac_before[n_units_u])
            pool.wait_ge(o_psum, 2 * (HEADS - 1))
            pool.wait_ge(qk_ready, 16 * (HEADS - 1) + 2)
            for g, w in enumerate(WINDOWS):
                steps = w.bit_length() - 1
                ug = u_T[:, g, :].rearrange("p (r w) -> p r w", w=GRID_W)
                src, dst = box
                wide = GRID_W + 2 * PAD
                a = src[:, 0:GRID_H * wide].rearrange("p (r w) -> p r w", w=wide)
                link(G.memset(src[:], 0.0))
                link(G.tensor_copy(a[:, :, PAD:PAD + GRID_W], ug))
                for s in range(steps):
                    k = 1 << s
                    if s < steps - 1:
                        b = dst[:, 0:GRID_H * wide].rearrange("p (r w) -> p r w", w=wide)
                        link(G.tensor_tensor(b[:, :, 0:wide - 2 * k + 1], a[:, :, 0:wide - 2 * k + 1],
                                             a[:, :, k:wide - k + 1], ALU.add))
                    else:
                        b = dst[:].rearrange("p (r w) -> p r w", w=GRID_W)
                        link(G.memset(dst[:], 0.0))
                        o = PAD - w // 2
                        link(G.tensor_tensor(b[:, PAD:PAD + GRID_H, :], a[:, :, o:o + GRID_W],
                                             a[:, :, o + k:o + k + GRID_W], ALU.add))
                    a = b
                    src, dst = dst, src
                rows = GRID_H + 2 * PAD
                for s in range(steps):
                    k = 1 << s
                    b = dst[:].rearrange("p (r w) -> p r w", w=GRID_W)
                    if s < steps - 1:
                        link(G.tensor_tensor(b[:, 0:rows - 2 * k + 1, :], a[:, 0:rows - 2 * k + 1, :],
                                             a[:, k:rows - k + 1, :], ALU.add))
                    else:
                        o = PAD - w // 2
                        link(G.tensor_tensor(b[:, 0:GRID_H, :], a[:, o:o + GRID_H, :],
                                             a[:, o + k:o + k + GRID_H, :], ALU.add))
                    a = b
                    src, dst = dst, src
                m = a[:, 0:GRID_H, :]
                link(G.tensor_tensor(m, m, cnt_r[:, g, :].unsqueeze(2).to_broadcast([P, GRID_H, GRID_W]), ALU.mult))
                link(G.tensor_tensor(m, m, cnt_c[:, g, :].unsqueeze(1).to_broadcast([P, GRID_H, GRID_W]), ALU.mult))
                G.tensor_tensor(ug, m, ug, ALU.subtract).then_inc(box_used, 1)
                pool.wait_ge(box_used, g + 1)

            pool.wait_ge(o_ready, 2 * HEADS)
            pool.wait_ge(diag_used, 2 * KT)
            G.iota(slot_ids[:], pattern=[[1, BLOCK]], base=0, channel_multiplier=0,
                   allow_small_or_imprecise_dtypes=True).then_inc(ids_ready, 1)
            pool.wait_ge(zero_ready, 1)
            for b in range(Y_ZERO):
                for k in range(2):
                    row = (2 * b + k) * P
                    pool.dma_start(y_dram[row:row + P, :], yrow[:, k, :]).then_inc(y_added[k], 16)

            for k in range(2):
                pool.wait_ge(xn2_out[k], 16 * TL // 2)
            pool.wait_ge(tables, 1)
            pool.dma_start(xg[0:1, 1, :], xn_dram[0:1, :]).then_inc(xg_in[1], 16)
            pool.wait_ge(xg_in[1], 16)
            n_items = loop_count(pool)
            pool.wait_ge(idx_ready, 1)
            v_next = item_variant(pool, 0)

            def gathers(v):
                G.indirect_dma_start(xg[:, 0, :], None, xn_dram,
                                     bass.IndirectOffsetOnAxis(ap=gidx[:, 0:1], axis=0)).then_inc(xg_in[0], 16)
                with pool.If(v > 2):
                    G.indirect_dma_start(xg[:, 1, :], None, xn_dram,
                                         bass.IndirectOffsetOnAxis(ap=gidx[:, 1:2], axis=0)).then_inc(xg_in[1], 16)

            gathers(v_next)
            with pool.Fori(0, n_items) as i:
                v = item_variant(pool, i)
                v1 = item_variant(pool, i + 1)
                h = large_before(pool, i)
                pool.wait_ge(y_added[0], i * 16 + 16 * Y_ZERO)
                pool.wait_ge(y_added[1], h * 16 + 16 * Y_ZERO)
                apart(pool)
                G.tensor_copy(sidx_cur[:], sidx[:]).then_inc(sidx_copied, 1)
                pool.wait_ge(idx_ready, i + 2)
                pool.wait_ge(xT_psum, i * 4 + 4)
                apart(pool)
                gathers(v1)
                pool.wait_ge(sidx_copied, i + 1)
                pool.wait_ge(yr_ready, i * 2 + 4)
                apart(pool)
                G.indirect_dma_start(y_dram, bass.IndirectOffsetOnAxis(ap=sidx_cur[:, 0:1], axis=0), yrow[:, 0, :],
                                     None, compute_op=ALU.add).then_inc(y_added[0], 16)
                with pool.If(v > 2):
                    G.indirect_dma_start(y_dram, bass.IndirectOffsetOnAxis(ap=sidx_cur[:, 1:2], axis=0),
                                         yrow[:, 1, :], None, compute_op=ALU.add).then_inc(y_added[1], 16)

        @block.scalar
        def _(act):
            A = nc.scalar
            count = [0]

            def link(ins):
                count[0] += 1
                ins.then_inc(act_chain, 1)
                act.wait_ge(act_chain, count[0])

            def root(n, lo, hi):
                act.wait_ge(var_ready, n + 1)
                A.activation(rs_s[:, lo:hi], rs_v[:, lo:hi], ACT.Sqrt).then_inc(root_ready, 1)

            act.wait_ge(x_in, 16)
            for t in range(NT):
                if t == TL:
                    act.wait_ge(ctx_in, 16)
                ins = A.activation(junk[:], x_all[:, t, :], ACT.Square, accum_out=ssq[:, t:t + 1])
                if t < NT - 1:
                    link(ins)
            ins.then_inc(sq_done, 1)
            root(0, 0, NT)
            act.wait_ge(vec_sb, 1)
            A.activation(sigc[:], vecT[:, V_C:V_C + 2 * KT], ACT.Sigmoid).then_inc(cond_sig, 1)
            act.wait_ge(lb_diff, 1)
            A.activation(lbT[:, 0, :], lbd[:], ACT.Sigmoid)
            A.activation(lbT[:, 1, :], lbd[:], ACT.Sigmoid, scale=-1.0).then_inc(lb_ready, 1)
            act.wait_ge(mod_ready, 1)
            for g, (k, t0, nt, s) in enumerate(XGROUPS):
                if g % 2 == 0:
                    act.wait_ge(xt0_psum, g + 1)
                    A.activation(hxT[:, k, t0 * P:(t0 + nt) * P], ps[:, g % 5, 0:nt * P], ACT.Identity,
                                 bias=mod[:, k, s:s + 1], scale=A1[:, k, s:s + 1]).then_inc(xt0_act, 1)

            def evacuate(us):
                for ui in us:
                    kind, *a = units[ui]
                    if kind == "a":
                        continue
                    n = evac_before[ui]
                    act.wait_ge(proj_psum, n + 1)
                    b = ps[:, n % 3, :]
                    if kind == "v":
                        t, h2 = a[:2]
                        A.copy(v_tok[:, t, h2 * QW:(h2 + 1) * QW], b[:, 0:QW]).then_inc(proj_evac, 1)
                    elif kind == "g":
                        t, h2 = a[:2]
                        A.activation(sig_g[:, t, h2 * QW:(h2 + 1) * QW], b[:, 0:QW], ACT.Sigmoid
                                     ).then_inc(proj_evac, 1)
                    elif kind == "f":
                        h, d, part = a[:3]
                        if h >= 1 and d == 0 and part == 0:
                            act.wait_ge(qk_ready, 16 * (h - 1) + 2)
                        lo, hi = ((0, 512), (512, SEQ), (SEQ, TOK))[part]
                        A.activation(sig_f[d][:, lo:hi], b[:, 0:hi - lo], ACT.Sigmoid)
                        A.activation(sig_k[d][:, lo:hi], b[:, 0:hi - lo], ACT.Sigmoid, scale=-1.0
                                     ).then_inc(proj_evac, 1)
                    elif kind == "q":
                        h, _, part = a[:3]
                        if h >= 1 and part == 0:
                            act.wait_ge(diag_psum, 2 * h)
                        A.activation(q_s[:, part * 512:part * 512 + 512], b, ACT.Sigmoid)
                        A.copy(q_raw[:, part * 512:part * 512 + 512], b).then_inc(proj_evac, 1)
                    elif kind == "u":
                        g, part = a[:2]
                        if g == 0 and part == 0:
                            act.wait_ge(qk_ready, 16 * (HEADS - 1) + 2)
                            act.wait_ge(diag_psum, 2 * HEADS)
                        A.copy(u_T[:, g, part * 512:part * 512 + 512], b).then_inc(proj_evac, 1)

            evacuate(range(n_ada_first, window[1]))
            for h in range(HEADS):
                for lv in range(LEVELS):
                    evacuate(head_units[h][lv])
                for j, (d, lo, hi) in enumerate(BATCHES):
                    act.wait_ge(kT_psum, 6 * h + j + 1)
                    if j >= 2 or h >= 1:
                        act.wait_ge(u_psum, 6 * h + j - 1)
                    A.copy(kT_sb[j % 2][:, 0:(hi - lo) * P], ps[:, 5, 0:(hi - lo) * P]).then_inc(kT_ready, 1)
                    evacuate(head_units[h][LEVELS + j])
                for half in range(2):
                    act.wait_ge(o_psum, 2 * h + half + 1)
                    for k in range(4):
                        ch = 4 * half + k
                        link(A.activation(o_junk[:], ps[:, 5 + half, k * P:(k + 1) * P], ACT.Square,
                                          accum_out=ssq[:, ch * HEADS + h:ch * HEADS + h + 1]))
                    A.copy(o_tok[:, 4 * half:4 * half + 4, h * P:(h + 1) * P],
                           ps[:, 5 + half, :].rearrange("p (c v) -> p c v", v=P)).then_inc(o_ready, 1)
            root(1, 0, TL * HEADS)
            act.wait_ge(proj_psum, evac_before[-1])
            for h in range(HEADS):
                for half in range(2):
                    n = 2 * h + half
                    act.wait_ge(oT_psum, n + 1)
                    A.activation(mixT[:, h, half * 512:half * 512 + 512], ps[:, 3 + n % 2, :], ACT.Copy,
                                 scale=vecT[:, V_NORM + h:V_NORM + h + 1]).then_inc(mix_ready, 1)
            for g in range(NG):
                for half in range(2):
                    n = 2 * HEADS + 2 * g + half
                    act.wait_ge(oT_psum, n + 1)
                    A.activation(mixT[:, HEADS + g, half * 512:half * 512 + 512], ps[:, 3 + n % 2, :], ACT.Copy,
                                 scale=vecT[:, V_SCALE + g:V_SCALE + g + 1]).then_inc(mix_ready, 1)
            for k in range(2):
                for half in range(2):
                    n = 2 * k + half
                    act.wait_ge(diag_used, 4 * (n + 1))
                    A.copy(gain[k][:, half * HALF:(half + 1) * HALF], ps[:, 5 + n % 2, :]).then_inc(gain_ready, 1)
            def transposed_tile(t):
                act.wait_ge(xt2_psum, t + 1)
                if t >= 2:
                    act.wait_ge(logit_psum, t - 1)
                for k in range(KT):
                    last = A.activation(hx2T[t % 2][:, k, :], ps[:, 4 + k // 4, (k % 4) * P:(k % 4 + 1) * P],
                                        ACT.Identity, bias=mod[:, 3 * KT + k, 0:1], scale=A2[:, k:k + 1])
                last.then_inc(xt2_ready, 1)

            for t in range(TL):
                b = 2 * (t % 2)
                act.wait_ge(yx_psum, t + 1)
                A.activation(wide_t[:], ps[:, b:b + 2, :].rearrange("p a n -> p (a n)"), ACT.Square,
                             accum_out=ssq[:, 0:1]).then_inc(sq_done, 1)
                root(2 + 2 * t, 0, 1)
                act.wait_ge(yx_used, t + 1)
                if t >= 2:
                    act.wait_ge(xn2_out[t % 2], 16 * (t // 2))
                    act.wait_ge(xt2_psum, t - 1)
                A.activation(xn_t[t % 2][:], x1[:, t, :], ACT.Square, accum_out=ssq[:, 0:1]).then_inc(sq_done, 1)
                root(3 + 2 * t, 0, 1)
                if t >= 1:
                    transposed_tile(t - 1)
            transposed_tile(TL - 1)
            for n in range(2):
                act.wait_ge(bt_psum, n + 1)
                w = 3 * KT * NE // 2
                A.copy(biasT[:].rearrange("p a e -> p (a e)")[:, n * w:(n + 1) * w], ps[:, 4 + n, 0:w]
                       ).then_inc(bt_ready, 1)
            act.wait_ge(top_diff, 1)
            A.activation(w_route[:], w_route[:], ACT.Exp).then_inc(top_exp, 1)

            def evacuate_xT(v, n_item):
                N = STEP * v
                for q in range(4):
                    act.wait_ge(xT_psum, n_item * 4 + (q + 1))
                    for k in (2 * q, 2 * q + 1):
                        last = A.activation(xT[:, k, 0:N], ps[:, (5, 6, 7, 5)[q], (k % 2) * BLOCK:(k % 2) * BLOCK + N],
                                            ACT.Identity, bias=mod[:, 3 * KT + k, 0:1], scale=A2[:, k:k + 1])
                    last.then_inc(xT_ready, 1)

            act.wait_ge(tables, 1)
            base = count[0]
            n_items = loop_count(act)
            v0 = item_variant(act, 0)
            for v in VARIANTS:
                with act.If(v0 == v):
                    evacuate_xT(v, 0)
            act.sem_inc(yr_ready, 2)
            with act.Fori(0, n_items) as i:
                e = item_expert(act, i)
                vi = item_variant(act, i)
                vn = item_variant(act, i + 1)
                h = large_before(act, i)
                A.copy(bias_d[:], biasT[:, 2 * KT:3 * KT, bass.ds(e, 1)].rearrange("p a o -> p (a o)")
                       ).then_inc(act_chain, 1)
                act.wait_ge(idx_ready, i + 1)
                act.wait_ge(yr_ready, i * 2 + 2)
                A.copy(w_cur[:], w_next[:]).then_inc(w_copied, 1)
                for v in VARIANTS:
                    with act.If(vi == v):
                        N = STEP * v
                        for j in range(KT):
                            act.wait_ge(gate_ready, i * KT + (j + 1))
                            A.activation(sig_sb[j % 2][:, 0:N], gate_sb[j % 2][:, 0:N], ACT.Sigmoid,
                                         scale=SWIGLU_ALPHA).then_inc(sig_ready, 1)
                for v in VARIANTS:
                    with act.If(vn == v):
                        evacuate_xT(v, i + 1)
                act.wait_ge(act_chain, i + (base + 1))
                act.wait_ge(w_copied, i + 1)
                act.wait_ge(y_added[0], i * 16 + 16 * Y_ZERO)
                act.wait_ge(y_added[1], h * 16 + 16 * Y_ZERO)
                apart(act)
                for v in VARIANTS:
                    with act.If(vi == v):
                        N = STEP * v
                        for j in range(KT + 1):
                            if j < KT:
                                act.wait_ge(d_psum, i * KT + (j + 1))
                                A.activation(yT[:, j, 0:N], ps[:, 3 + j % 2, 0:N], ACT.Identity,
                                             bias=bias_d[:, j:j + 1]).then_inc(yT_ready, 1)
                            if j in (4, KT):
                                half = 0 if j == 4 else 1
                                act.wait_ge(yr_psum, i * 2 + (half + 1))
                                for s in range((N + P - 1) // P):
                                    m = min(P, N - s * P)
                                    last = A.activation(yrow[0:m, s, half * HALF:(half + 1) * HALF],
                                                        ps[0:m, ((6, 7), (5, 6))[half][s], :], ACT.Copy,
                                                        scale=w_cur[0:m, s:s + 1])
                                last.then_inc(yr_ready, 1)
            for t in range(TL):
                act.wait_ge(y_in[t % 2], 16 * (t // 2 + 1))
                A.activation(wide_t[:], xn_t[t % 2][:], ACT.Square, accum_out=ssq[:, 0:1]).then_inc(fin_sq, 1)
                root(2 + 2 * TL + t, 0, 1)

        @block.vector
        def _(dve):
            V = nc.vector
            count = [0]

            def link(ins):
                count[0] += 1
                ins.then_inc(dve_chain, 1)
                dve.wait_ge(dve_chain, count[0])

            n_root = [0]

            def rsqrt(n, lo, hi, width):
                n = n_root[0]
                n_root[0] += 1
                c_ = slice(lo, hi)
                V.tensor_scalar(rs_v[:, c_], ssq[:, c_], 1.0 / width, EPS, ALU.mult, ALU.add).then_inc(var_ready, 1)
                dve.wait_ge(root_ready, n + 1)
                link(V.reciprocal(rs_s[:, c_], rs_s[:, c_]))
                link(V.tensor_tensor(rs_t[:, c_], rs_s[:, c_], rs_s[:, c_], ALU.mult))
                link(V.tensor_tensor(rs_t[:, c_], rs_t[:, c_], rs_v[:, c_], ALU.mult))
                link(V.tensor_scalar(rs_t[:, c_], rs_t[:, c_], -0.5, 1.5, ALU.mult, ALU.add))
                link(V.tensor_tensor(rstd[:, c_], rs_s[:, c_], rs_t[:, c_], ALU.mult))

            dve.wait_ge(vec_psum, 1)
            V.tensor_copy(vecT[:], ps[:, 7, 0:120]).then_inc(vec_sb, 1)
            dve.wait_ge(vec_sb, 1)
            V.tensor_tensor(lbd[:], vecT[:, V_LB:V_LB + 2 * HEADS], vecT[:, V_LB + 2 * HEADS:V_LB + 4 * HEADS],
                            ALU.subtract).then_inc(lb_diff, 1)
            dve.wait_ge(sq_done, 1)
            rsqrt(0, 0, NT, D)
            dve.wait_ge(cond_sig, 1)
            for s in range(2):
                last = V.tensor_tensor(cT[:, :, s], vecT[:, V_C + s * KT:V_C + (s + 1) * KT], sigc[:, s, :], ALU.mult)
            last.then_inc(cond_ready, 1)
            for t in range(NT):
                V.tensor_scalar(x_all[:, t, :], x_all[:, t, :], rstd[:, t:t + 1], None, ALU.mult
                                ).then_inc(xn_ready, 1)
            dve.wait_ge(ada_psum, n_ada_first)
            n2 = 2 * KT

            def bc(v, lo, n, m):
                return v[:, lo:lo + n].unsqueeze(2).to_broadcast([P, n, m])

            link(V.tensor_tensor(mod[:, 0:n2, :], ps[:, 7, 0:2 * n2].rearrange("p (n s) -> p n s", s=2),
                                 bc(vecT, V_BADA, n2, 2), ALU.add))
            V.scalar_tensor_tensor(out=A1[:], in0=mod[:, KT:n2, :], scalar=1.0, in1=bc(vecT, V_GPM, KT, 2),
                                   op0=ALU.add, op1=ALU.mult).then_inc(mod_ready, 1)
            dve.wait_ge(mod_ready, 1)
            for g, (k, t0, nt, s) in enumerate(XGROUPS):
                if g % 2 == 1:
                    dve.wait_ge(xt0_psum, g + 1)
                    V.tensor_scalar(hxT[:, k, t0 * P:(t0 + nt) * P], ps[:, g % 5, 0:nt * P], A1[:, k, s:s + 1],
                                    mod[:, k, s:s + 1], ALU.mult, ALU.add).then_inc(xt0_dve, 1)
            dve.wait_ge(consts, 2)
            link(V.reciprocal(cnt_c[:], cnt_c[:]))
            link(V.reciprocal(cnt_r[:], cnt_r[:]))
            dve.wait_ge(lb_ready, 1)
            dve.wait_ge(xt0_psum, len(XGROUPS))
            V.memset(att[0][:], 0.0)
            V.memset(att[1][:], 0.0)

            def blocks(v, h, half, lo=0, n=SEQ):
                return v[:, lo:lo + n].rearrange("p (b two j) -> p b two j", two=2, j=h)[:, :, half, :]

            def firsts(v, h, half, n):
                return v[:, 0:n].rearrange("p (b two j) -> p b two j", two=2, j=h)[:, :, half, 0:1].to_broadcast(
                    [P, n // (2 * h), h])

            for h in range(HEADS):
                dve.wait_ge(proj_evac, evac_before[window[h + 1]])
                if h:
                    dve.wait_ge(o_psum, 2 * h)
                link(V.tensor_tensor(q_s[:], q_s[:], q_raw[:], ALU.mult))
                for d in range(2):
                    col = d * HEADS + h
                    V.tensor_scalar(Fd[d][:], sig_f[d][:], lbT[:, 1, col:col + 1], lbT[:, 0, col:col + 1],
                                    ALU.mult, ALU.add)
                    link(V.tensor_scalar(Kd[d][:], sig_k[d][:], lbT[:, 1, col:col + 1], None, ALU.mult))
                for d in range(2):
                    V.tensor_tensor(Qd[d][:], q_s[:], Fd[d][:, 0:SEQ], ALU.mult).then_inc(qk_ready, 1)
                a = att[h % 2]
                for half in range(2):
                    dve.wait_ge(diag_psum, 2 * h + half + 1)
                    V.copy_predicated(a[:, 4 * half:4 * half + 4, :],
                                      ident[:].bitcast(U32).unsqueeze(1).to_broadcast([P, 4, P]),
                                      ps[:, 5 + half, :].rearrange("p (c t) -> p c t", t=P)).then_inc(diag_put, 1)
                dve.wait_ge(diag_put, 2 * h + 2)
                for lv in range(LEVELS):
                    w = 1 << lv
                    nb = P // (2 * w)
                    for d in range(2):
                        dve.wait_ge(lev_psum, 2 * (h * LEVELS + lv) + d + 1)
                        for part in range(2):
                            cs = slice(4 * part, 4 * part + 4)
                            mk = masks[:, d, lv, :]
                            last = V.copy_predicated(
                                a[:, cs, :].rearrange("p c (b two j) -> p c b two j", two=2, j=w)[:, :, :, 1 - d, :],
                                mk.bitcast(U32).rearrange("p (b j) -> p b j", j=w).unsqueeze(1).to_broadcast(
                                    [P, 4, nb, w]),
                                ps[:, 3 + d, part * 256:part * 256 + 256].rearrange("p (c b j) -> p c b j", c=4, j=w))
                        last.then_inc(lev_put, 1)
                        q_half, k_half = (1, 0) if d == 0 else (0, 1)
                        V.tensor_tensor(blocks(Qd[d], w, q_half), blocks(Qd[d], w, q_half),
                                        firsts(Fd[d], w, 1 - q_half, SEQ), ALU.mult)
                        link(V.tensor_tensor(blocks(Kd[d], w, k_half, 0, TOK), blocks(Kd[d], w, k_half, 0, TOK),
                                             firsts(Fd[d], w, 1 - k_half, TOK), ALU.mult))
                        f = Fd[d][:, 0:TOK].rearrange("p (b two j) -> p b two j", two=2, j=w)
                        V.tensor_tensor(f[:, :, 0, 0:1], f[:, :, 0, 0:1], f[:, :, 1, 0:1], ALU.mult
                                        ).then_inc(qk_ready, 1)
                        dve.wait_ge(qk_ready, 16 * h + 2 * lv + d + 3)
                for j, (d, lo, hi) in enumerate(BATCHES):
                    dve.wait_ge(u_psum, 6 * h + j + 1)
                    for n in range(lo, hi):
                        u = ps[:, 6, (n - lo) * P:(n - lo + 1) * P]
                        s_new = states[d][:, state_slot(n), :]
                        if n == 0:
                            ins = V.tensor_copy(s_new, u)
                        else:
                            ch = SCAN[d][n]
                            ins = V.scalar_tensor_tensor(out=s_new, in0=states[d][:, state_slot(n - 1), :],
                                                         scalar=Fd[d][:, ch * P:ch * P + 1], in1=u,
                                                         op0=ALU.mult, op1=ALU.add)
                        if n < hi - 1:
                            link(ins)
                    ins.then_inc(state_ready, 1)
                    dve.wait_ge(state_ready, 6 * h + j + 1)
            dve.wait_ge(o_ready, 2 * HEADS)
            rsqrt(1, 0, TL * HEADS, P)
            dve.wait_ge(proj_evac, evac_before[-1])
            for h in range(HEADS):
                for t in range(TL):
                    o = o_tok[:, t, h * P:(h + 1) * P]
                    last = V.scalar_tensor_tensor(out=o, in0=o, scalar=rstd[:, t * HEADS + h:t * HEADS + h + 1],
                                                  in1=sig_g[:, t, h * P:(h + 1) * P], op0=ALU.mult, op1=ALU.mult)
                    if t % 4 == 3:
                        last.then_inc(gated, 1)
            dve.wait_ge(ada_psum, 6 * KT)
            link(V.tensor_tensor(mod[:, n2:, :], ps[:, 7, 2 * n2:12 * KT].rearrange("p (n s) -> p n s", s=2),
                                 bc(vecT, V_BADA + n2, 4 * KT, 2), ALU.add))
            V.tensor_tensor(gpost[:, 0, :], mod[:, 2 * KT:3 * KT, 0], vecT[:, V_GQM:V_GQM + KT], ALU.mult)
            V.tensor_tensor(gpost[:, 1, :], mod[:, 5 * KT:6 * KT, 0], vecT[:, V_GQF:V_GQF + KT], ALU.mult)
            link(V.scalar_tensor_tensor(out=A2[:], in0=mod[:, 4 * KT:5 * KT, 0], scalar=1.0,
                                        in1=vecT[:, V_GPF:V_GPF + KT], op0=ALU.add, op1=ALU.mult))
            for n in range(2 * KT):
                if n:
                    dve.wait_ge(diag_used, n)
                V.tensor_scalar(diag_t[:], ident[:], gpost[:, n // KT, n % KT:n % KT + 1], None, ALU.mult
                                ).then_inc(diag_ready, 1)
            dve.wait_ge(gain_ready, 4)
            dve.wait_ge(x1_in, 16)
            for t in range(TL):
                b = 2 * (t % 2)
                dve.wait_ge(sq_done, 2 + 2 * t)
                rsqrt(2 + 2 * t, 0, 1, D)
                yx = ps[:, b:b + 2, :].rearrange("p a n -> p (a n)")
                link(V.scalar_tensor_tensor(out=wide_t[:], in0=yx, scalar=rstd[:, 0:1], in1=gain[0][:],
                                            op0=ALU.mult, op1=ALU.mult))
                V.tensor_tensor(x1[:, t, :], x1[:, t, :], wide_t[:], ALU.add).then_inc(yx_used, 1)
                dve.wait_ge(sq_done, 3 + 2 * t)
                rsqrt(3 + 2 * t, 0, 1, D)
                if t >= 2:
                    dve.wait_ge(xn2_out[t % 2], 16 * (t // 2))
                    dve.wait_ge(xt2_psum, t - 1)
                V.tensor_scalar(xn_t[t % 2][:], x1[:, t, :], rstd[:, 0:1], None, ALU.mult).then_inc(xn2_ready, 1)
            dve.wait_ge(gated, 2 * HEADS)
            dve.wait_ge(oT_psum, 2 * HEADS)
            V.memset(yrow[:], 0.0).then_inc(zero_ready, 1)

            dve.wait_ge(logit_psum, TL)
            link(V.tensor_copy(logit[:], ps[:, 6, 0:TL * NE].rearrange("p (t e) -> p t e", e=NE)))
            for t in range(TL):
                link(V.max(top_v[:, t, :], logit[:, t, :]))
                link(V.max_index(top_i[:, t, :], top_v[:, t, :], logit[:, t, :]))
            link(V.tensor_copy(top_f[:], top_i[:]))
            V.tensor_tensor(w_route[:], top_v[:, :, 0:TOP_K], top_v[:, :, 0:1].to_broadcast([P, TL, TOP_K]),
                            ALU.subtract).then_inc(top_diff, 1)
            dve.wait_ge(top_exp, 1)
            link(V.tensor_reduce(out=row_t[:, 0, :], in_=w_route[:], axis=AX_X, op=ALU.add))
            link(V.reciprocal(row_t[:, 0, :], row_t[:, 0, :]))
            link(V.tensor_tensor(w_route[:], w_route[:],
                                 row_t[:, 0, :].unsqueeze(2).to_broadcast([P, TL, TOP_K]), ALU.mult))
            link(V.memset(mask[:], 0.0))
            link(V.memset(rtab[:], 0.0))
            e_grid = iota_e[:].unsqueeze(1).to_broadcast([P, TL, NE])
            for j in range(TOP_K):
                link(V.tensor_tensor(onehot[:], e_grid, top_f[:, :, j:j + 1].to_broadcast([P, TL, NE]), ALU.is_equal))
                link(V.tensor_tensor(mask[:], mask[:], onehot[:], ALU.add))
                link(V.tensor_tensor(wtmp[:], onehot[:], w_route[:, :, j:j + 1].to_broadcast([P, TL, NE]), ALU.mult))
                link(V.tensor_tensor(rtab[:, :, 2:], rtab[:, :, 2:], wtmp[:], ALU.add))
            V.tensor_copy(mask_bf[:], mask[:]).then_inc(mask_ready, 1)
            link(V.tensor_reduce(out=row_t[:, 1, 0:1], in_=upper_f[:], axis=AX_X, op=ALU.add))
            link(V.tensor_scalar(row_t[:, 1, 0:1], row_t[:, 1, 0:1], -1.0, float(P - 1), ALU.mult, ALU.add))
            for t in range(TL):
                V.tensor_scalar(rtab[:, t, 0:1], row_t[:, 1, 0:1], float(t * P), None, ALU.add)
                link(V.tensor_scalar(rtab[:, t, 1:2], row_t[:, 1, 0:1], 0.0, 1.0, ALU.mult, ALU.add))
            dve.wait_ge(pos_psum, 1)
            link(V.tensor_copy(cnt[:], ps[:, 6, 0:NE]))
            link(V.scalar_tensor_tensor(out=pos[:], in0=ps[:, 5, 0:TL * NE].rearrange("p (t e) -> p t e", e=NE),
                                        scalar=FAR, in1=mask[:], op0=ALU.add, op1=ALU.mult))
            link(V.tensor_scalar(pos[:], pos[:], -FAR, None, ALU.add))
            NC = NE * CHUNKS

            def grid(v):
                return v[:].rearrange("p (e c) -> p e c", c=CHUNKS)

            for k in range(CHUNKS):
                V.tensor_scalar(grid(cand_has)[:, :, k], cnt[:], float(BLOCK * (k + 1)), None, ALU.is_gt)
                V.tensor_scalar(grid(cand_b)[:, :, k], iota_e[:], 0.0, float(BLOCK * (k + 1)), ALU.mult, ALU.add)
                V.tensor_copy(grid(cand_e)[:, :, k], iota_e[:])
                link(V.tensor_copy(grid(cand_c)[:, :, k], cnt[:]))
            link(V.tensor_scalar(cand_v[:, 0, :], cand_has[:], 0.0, 1.0, ALU.mult, ALU.add))
            link(V.tensor_tensor_scan(cand_rank[:], cand_v[:, 0, :], cand_has[:], 0.0, ALU.mult, ALU.add))
            link(V.tensor_scalar(n_items_f[:, 0:1], cand_rank[:, NC - 1:NC], float(NE), None, ALU.add))
            link(V.tensor_tensor(cand_rank[:], cand_rank[:], cand_has[:], ALU.mult))
            for j in range(OVER):
                last = V.tensor_scalar(cand_oh[:, j, :], cand_rank[:], float(j + 1), None, ALU.is_equal)
            link(last)
            link(V.tensor_copy(tab_e[:, 0:NE], iota_e[:]))
            link(V.memset(tab_c[:], 0.0))
            link(V.tensor_copy(tab_c[:, 0:NE], cnt[:]))
            for src, dst in ((cand_e, tab_e), (cand_b, tab_b), (cand_c, tab_c)):
                link(V.tensor_tensor(cand_v[:], cand_oh[:], src[:].unsqueeze(1).to_broadcast([P, OVER, NC]), ALU.mult))
                link(V.tensor_reduce(out=dst[:, NE:NE + OVER], in_=cand_v[:], axis=AX_X, op=ALU.add))
            link(V.tensor_tensor(tab_c[:], tab_c[:], tab_b[:], ALU.subtract))
            link(V.tensor_scalar(tab_v[:], tab_c[:], 0.0, 1.0, ALU.mult, ALU.add))
            for k in range(1, len(VARIANTS)):
                link(V.scalar_tensor_tensor(out=tab_v[:], in0=tab_c[:], scalar=float(STEP * k), in1=tab_v[:],
                                            op0=ALU.is_gt, op1=ALU.add))
            link(V.tensor_copy(int_v[:], tab_v[:]))
            link(V.tensor_copy(int_e[:], tab_e[:]))
            link(V.tensor_scalar(tab_c[:], tab_v[:], float(P // STEP), None, ALU.is_gt))
            link(V.tensor_tensor_scan(tab_v[:], ones[:, 0:NTAB], tab_c[:], 0.0, ALU.mult, ALU.add))
            V.memset(int_h[:, 0:1], 0)
            link(V.tensor_copy(int_h[:, 1:NTAB], tab_v[:, 0:NTAB - 1]))
            V.tensor_copy(int_n[:, 0:1], n_items_f[:, 0:1]).then_inc(tables, 1)
            dve.wait_ge(tables, 1)
            base = count[0]
            n_items = loop_count(dve)

            def build_sel(i, lk):
                e = item_expert(dve, i)
                V.tensor_copy(posc[:], pos[:, :, bass.ds(e, 1)].rearrange("p t o -> p (t o)"))
                lk(V.tensor_scalar(iota_b[:], slot_ids[:], tab_b[:, bass.ds(i, 1)], None, ALU.add))
                for t in range(TL):
                    last = V.tensor_scalar(sel[:, t, :], iota_b[:], posc[:, t:t + 1], None, ALU.is_equal)
                last.then_inc(sel_ready, 1)

            def slots(i, lk):
                e = item_expert(dve, i)
                t3 = ps[:, 7, 0:2 * (NE + 2)].rearrange("p (s n) -> p s n", s=2)
                V.tensor_copy(gidx[:], t3[:, :, 0])
                V.tensor_copy(w_next[:], t3[:, :, bass.ds(e + 2, 1)].rearrange("p s o -> p (s o)"))
                lk(V.tensor_tensor(sidx_f[:], t3[:, :, 1], spare[:], ALU.mult))
                lk(V.tensor_tensor(sidx_f[:], spare[:], sidx_f[:], ALU.subtract))
                V.tensor_tensor(sidx[:], sidx_f[:], t3[:, :, 0], ALU.add).then_inc(idx_ready, 1)

            dve.wait_ge(ids_ready, 1)
            build_sel(0, link)
            dve.wait_ge(sel_psum, 1)
            slots(0, link)
            build_sel(1, link)
            base = count[0]
            LOOP_LINKS = 2 * KT + 4

            with dve.Fori(0, n_items) as i:
                e = item_expert(dve, i)
                vi = item_variant(dve, i)
                h = large_before(dve, i + 1)

                def swiglu(js, v, lk):
                    N = STEP * v
                    for j in js:
                        dve.wait_ge(gu_psum, i * KT + (j + 1))
                        b = ps[:, j % 3, :]
                        g, u = gate_sb[j % 2][:, 0:N], up_sb[j % 2][:, 0:N]
                        V.tensor_scalar(g, b[:, 0:N], bias_gu[:, j:j + 1], SWIGLU_LIMIT, ALU.add, ALU.min
                                        ).then_inc(gate_ready, 1)
                        V.tensor_scalar(u, b[:, BLOCK:BLOCK + N], bias_gu[:, KT + j:KT + j + 1], SWIGLU_LIMIT,
                                        ALU.add, ALU.min).then_inc(gu_evac, 1)
                        dve.wait_ge(gu_evac, i * KT + (j + 1))
                        lk(V.tensor_scalar(u, u, -SWIGLU_LIMIT, 1.0, ALU.max, ALU.add))
                        lk(V.tensor_tensor(u, u, g, ALU.mult))
                        dve.wait_ge(sig_ready, i * KT + (j + 1))
                        V.tensor_tensor(hT[:, j, 0:N], u, sig_sb[j % 2][:, 0:N], ALU.mult).then_inc(h_ready, 1)

                def counter(start):
                    at = [start]

                    def lk(ins):
                        at[0] += 1
                        ins.then_inc(dve_chain, 1)
                        dve.wait_ge(dve_chain, i * LOOP_LINKS + (base + at[0]))

                    return lk

                counter(0)(V.tensor_copy(bias_gu[:], biasT[:, 0:2 * KT, bass.ds(e, 1)].rearrange("p a o -> p (a o)")))
                apart(dve)
                for v in VARIANTS:
                    with dve.If(vi == v):
                        swiglu(range(KT // 2), v, counter(1))
                dve.wait_ge(w_copied, i + 1)
                dve.wait_ge(sidx_copied, i + 1)
                dve.wait_ge(xg_in[0], i * 16 + 16)
                dve.wait_ge(xg_in[1], h * 16 + 16)
                dve.wait_ge(sel_psum, i + 2)
                slots(i + 1, counter(1 + KT))
                for v in VARIANTS:
                    with dve.If(vi == v):
                        swiglu(range(KT // 2, KT), v, counter(1 + KT + 2))
                build_sel(i + 2, counter(1 + 2 * KT + 2))
            done = n_items * LOOP_LINKS
            n_tail = [0]
            for t in range(TL):
                dve.wait_ge(fin_sq, t + 1)
                dve.wait_ge(y_in[t % 2], 16 * (t // 2 + 1))
                n = 2 + 2 * TL + t

                def lk(ins):
                    n_tail[0] += 1
                    ins.then_inc(dve_chain, 1)
                    dve.wait_ge(dve_chain, done + (base + n_tail[0]))

                V.tensor_scalar(rs_v[:, 0:1], ssq[:, 0:1], 1.0 / D, EPS, ALU.mult, ALU.add).then_inc(var_ready, 1)
                dve.wait_ge(root_ready, n + 1)
                lk(V.reciprocal(rs_s[:, 0:1], rs_s[:, 0:1]))
                lk(V.tensor_tensor(rs_t[:, 0:1], rs_s[:, 0:1], rs_s[:, 0:1], ALU.mult))
                lk(V.tensor_tensor(rs_t[:, 0:1], rs_t[:, 0:1], rs_v[:, 0:1], ALU.mult))
                lk(V.tensor_scalar(rs_t[:, 0:1], rs_t[:, 0:1], -0.5, 1.5, ALU.mult, ALU.add))
                lk(V.tensor_tensor(rstd[:, 0:1], rs_s[:, 0:1], rs_t[:, 0:1], ALU.mult))
                y = xn_t[t % 2][:]
                lk(V.scalar_tensor_tensor(out=y, in0=y, scalar=rstd[:, 0:1], in1=gain[1][:], op0=ALU.mult,
                                          op1=ALU.mult))
                V.tensor_tensor(x1[:, t, :], x1[:, t, :], y, ALU.add).then_inc(fin_ready, 1)

        @block.tensor
        def _(pe):
            T = nc.tensor
            pe.wait_ge(consts, 1)
            pe.wait_ge(vec_in, 160)
            T.transpose(ps[:, 7, 0:120], vec_rows[:], ident[0:120, 0:120]).then_inc(vec_psum, 1)
            pe.wait_ge(cond_ready, 1)
            pe.wait_ge(consts, 2)

            def run(us):
                for ui in us:
                    kind, *a = units[ui]
                    ch = a[-1]
                    if ui == 0 or units[ui - 1][-1] != ch:
                        uses = sum(len(chunks[n][0]) for n in range(ch % 3, ch + 1, 3))
                        pe.wait_ge(ring_in[ch % 3], 16 * uses)
                    w = ring[ch % 3]
                    n = evac_before[ui]
                    if kind != "a" and n >= 3:
                        pe.wait_ge(proj_evac, n - 2)
                    b = ps[:, n % 3, :]
                    for k in range(KT):
                        go = dict(start=k == 0, stop=k == KT - 1)
                        if kind == "a":
                            nt = a[0]
                            last = T.matmul(ps[:, 7, 2 * nt:2 * nt + 2], w[:, k, (nt % 2) * P:(nt % 2 + 1) * P],
                                            cT[:, k, :], **go)
                        elif kind in "vg":
                            t = a[0]
                            last = T.matmul(b[:, 0:QW], hxT[:, k, t * P:(t + 1) * P], w[:, k, :], **go)
                        elif kind == "f":
                            h, d, part = a[:3]
                            lo, hi = ((0, 512), (512, SEQ), (SEQ, TOK))[part]
                            last = T.matmul(b[:, 0:hi - lo], w[:, k, d * P:(d + 1) * P], hxT[:, k, lo:hi], **go)
                        elif kind == "q":
                            part = a[2]
                            last = T.matmul(b, w[:, k, 0:P], hxT[:, k, part * 512:part * 512 + 512], **go)
                        else:
                            g, part = a[:2]
                            last = T.matmul(b, w[:, k, (g % 2) * P:(g % 2 + 1) * P],
                                            hxT[:, k, part * 512:part * 512 + 512], **go)
                    last.then_inc(ada_psum if kind == "a" else proj_psum, 1)

            run(range(n_ada_first))
            for g, (k, t0, nt, s) in enumerate(XGROUPS):
                if g == 0:
                    pe.wait_ge(xn_ready, NT)
                if g >= 5:
                    o = g - 5
                    pe.wait_ge(xt0_act if o % 2 == 0 else xt0_dve, o // 2 + 1)
                for t in range(nt):
                    last = T.transpose(ps[:, g % 5, t * P:(t + 1) * P], x_all[:, t0 + t, k * P:(k + 1) * P], ident[:])
                last.then_inc(xt0_psum, 1)
            pe.wait_ge(xt0_act, len(XGROUPS) // 2)
            pe.wait_ge(xt0_dve, len(XGROUPS) // 2)
            pe.wait_ge(mod_ready, 1)
            run(range(n_ada_first, window[1]))
            for h in range(HEADS):
                a = att[h % 2]
                pe.wait_ge(qk_ready, 16 * h + 2)
                if h:
                    pe.wait_ge(o_ready, 2 * h)
                for half in range(2):
                    for k in range(4):
                        cs = slice((4 * half + k) * P, (4 * half + k + 1) * P)
                        for d in range(2):
                            last = T.matmul(ps[:, 5 + half, k * P:(k + 1) * P], Kd[d][:, cs], q_s[:, cs],
                                            start=d == 0, stop=d == 1)
                    last.then_inc(diag_psum, 1)
                for lv in range(LEVELS):
                    w = 1 << lv
                    for d in range(2):
                        pe.wait_ge(qk_ready, 16 * h + 2 * lv + d + 1)
                        if h or lv:
                            pe.wait_ge(lev_put, 2 * (h * LEVELS + lv) + d - 1)
                        for ch in range(TL):
                            cs = slice(ch * P, (ch + 1) * P)
                            q = Qd[d][:, cs].rearrange("p (b two j) -> p b two j", two=2, j=w)[:, :, 1 - d, :]
                            last = T.matmul(ps[:, 3 + d, ch * 64:(ch + 1) * 64], Kd[d][:, cs], q,
                                            start=True, stop=True)
                        last.then_inc(lev_psum, 1)
                    run(head_units[h][lv])
                for j, (d, lo, hi) in enumerate(BATCHES):
                    pe.wait_ge(qk_ready, 16 * h + 15 + d)
                    pe.wait_ge(diag_put, 2 * h + 2)
                    if j or h:
                        pe.wait_ge(kT_ready, 6 * h + j)
                    for n in range(lo, hi):
                        ch = SCAN[d][n]
                        last = T.transpose(ps[:, 5, (n - lo) * P:(n - lo + 1) * P], Kd[d][:, ch * P:(ch + 1) * P],
                                           ident[:])
                    last.then_inc(kT_psum, 1)
                    run(head_units[h][LEVELS + j])
                    pe.wait_ge(kT_ready, 6 * h + j + 1)
                    if j or h:
                        pe.wait_ge(state_ready, 6 * h + j)
                    for n in range(lo, hi):
                        ch = SCAN[d][n]
                        last = T.matmul(ps[:, 6, (n - lo) * P:(n - lo + 1) * P],
                                        kT_sb[j % 2][:, (n - lo) * P:(n - lo + 1) * P],
                                        v_tok[:, ch, h * P:(h + 1) * P], start=True, stop=True)
                    last.then_inc(u_psum, 1)
                pe.wait_ge(state_ready, 6 * h + 6)
                pe.wait_ge(lev_put, 2 * (h + 1) * LEVELS)
                for half in range(2):
                    for k in range(4):
                        ch = 4 * half + k
                        o = ps[:, 5 + half, k * P:(k + 1) * P]
                        T.matmul(o, a[:, ch, :], v_tok[:, ch, h * P:(h + 1) * P], start=True, stop=False)
                        T.matmul(o, Qd[0][:, ch * P:(ch + 1) * P], states[0][:, ch, :], start=False, stop=False)
                        last = T.matmul(o, Qd[1][:, ch * P:(ch + 1) * P], states[1][:, TL - 1 - ch, :],
                                        start=False, stop=True)
                    last.then_inc(o_psum, 1)
            pe.wait_ge(proj_evac, evac_before[-1])
            for h in range(HEADS):
                for half in range(2):
                    n = 2 * h + half
                    pe.wait_ge(gated, n + 1)
                    if n >= 2:
                        pe.wait_ge(mix_ready, n - 1)
                    for k in range(4):
                        last = T.transpose(ps[:, 3 + n % 2, k * P:(k + 1) * P],
                                           o_tok[:, 4 * half + k, h * P:(h + 1) * P], ident[:])
                    last.then_inc(oT_psum, 1)
            pe.wait_ge(misc_in, 48)
            for g in range(NG):
                pe.wait_ge(box_used, g + 1)
                for half in range(2):
                    n = 2 * HEADS + 2 * g + half
                    pe.wait_ge(mix_ready, n - 1)
                    T.matmul(ps[:, 3 + n % 2, :], pw_sb[:, g, :], u_T[:, g, half * 512:half * 512 + 512],
                             start=True, stop=True).then_inc(oT_psum, 1)
            pe.wait_ge(o_ready, 2 * HEADS)
            for n in range(2 * KT):
                pe.wait_ge(diag_ready, n + 1)
                if n >= 8 and n % 4 == 0:
                    pe.wait_ge(gain_ready, n // 4 - 1)
                T.matmul(ps[:, 5 + (n // 4) % 2, (n % 4) * P:(n % 4 + 1) * P], ones[:], diag_t[:], start=True,
                         stop=True).then_inc(diag_used, 1)
            pe.wait_ge(mix_ready, 4 * HEADS)
            pe.wait_ge(wo_in, 64)
            for t in range(TL + 2):
                if t < TL:
                    if t >= 2:
                        pe.wait_ge(yx_used, t - 1)
                    for q in range(NQ):
                        bank = 2 * (t % 2) + q // 2
                        for k in range(KT):
                            last = T.matmul(ps[:, bank, (q % 2) * QW:(q % 2 + 1) * QW], mixT[:, k, t * P:(t + 1) * P],
                                            wo_sb[q][:, k, :], start=k == 0, stop=k == KT - 1)
                    last.then_inc(yx_psum, 1)
                if 1 <= t <= TL:
                    pe.wait_ge(xn2_ready, t)
                    pe.wait_ge(gain_ready, 4)
                    if t >= 2:
                        pe.wait_ge(xt2_ready, t - 1)
                    for k in range(KT):
                        last = T.transpose(ps[:, 4 + k // 4, (k % 4) * P:(k % 4 + 1) * P],
                                           xn_t[(t - 1) % 2][:, k * P:(k + 1) * P], ident[:])
                    last.then_inc(xt2_psum, 1)
                if t >= 2:
                    pe.wait_ge(xt2_ready, t - 1)
                    lg = ps[:, 6, (t - 2) * NE:(t - 1) * NE]
                    for k in range(KT):
                        T.matmul(lg, hx2T[t % 2][:, k, :], wr_sb[:, k, :], start=k == 0, stop=False)
                    T.matmul(lg, ones[0:1, :], br_sb[:], start=False, stop=True).then_inc(logit_psum, 1)
            pe.wait_ge(brow_in, 48)
            pe.wait_ge(xt2_ready, TL)
            for m in range(3):
                for k in range(KT):
                    n = m * KT + k
                    b, o = divmod(n, 3 * KT // 2)
                    last = T.transpose(ps[:, 4 + b, o * NE:(o + 1) * NE], bias_rows[:, m, k * P:(k + 1) * P],
                                       ident[0:NE, 0:NE])
                    if o == 3 * KT // 2 - 1:
                        last.then_inc(bt_psum, 1)
            pe.wait_ge(mask_ready, 1)
            pe.wait_ge(bt_ready, 2)
            for t in range(TL):
                for j in range(t + 1):
                    T.matmul(ps[:, 5, t * NE:(t + 1) * NE], upper_bf[:] if j == t else ones_bf[:], mask_bf[:, j, :],
                             start=j == 0, stop=j == t)
            for t in range(TL):
                last = T.matmul(ps[:, 6, 0:NE], ones_bf[:], mask_bf[:, t, :], start=t == 0, stop=t == TL - 1)
            last.then_inc(pos_psum, 1)

            def slot_sums():
                for s in range(2):
                    for t in range(TL):
                        last = T.matmul(ps[:, 7, s * (NE + 2):(s + 1) * (NE + 2)], sel[:, t, s * P:(s + 1) * P],
                                        rtab[:, t, :], start=t == 0, stop=t == TL - 1)
                last.then_inc(sel_psum, 1)

            def transpose_rows(v, waits):
                N = STEP * v
                for q in range(4):
                    waits(q)
                    for k in (2 * q, 2 * q + 1):
                        for s in range((N + P - 1) // P):
                            m = min(P, N - s * P)
                            o = (k % 2) * BLOCK + s * P
                            last = T.transpose(ps[:, (5, 6, 7, 5)[q], o:o + m], xg[0:m, s, k * P:(k + 1) * P],
                                               ident[0:m, 0:m])
                    last.then_inc(xT_psum, 1)

            pe.wait_ge(sel_ready, 1)
            slot_sums()
            pe.wait_ge(tables, 1)
            n_items = loop_count(pe)
            v0 = item_variant(pe, 0)
            h0 = large_before(pe, 1)
            pe.wait_ge(idx_ready, 1)
            pe.wait_ge(xg_in[0], 16)
            pe.wait_ge(xg_in[1], h0 * 16 + 16)
            apart(pe)

            def first_waits(q):
                if q == 3:
                    pe.wait_ge(xT_ready, 1)

            for v in VARIANTS:
                with pe.If(v0 == v):
                    transpose_rows(v, first_waits)
            with pe.Fori(0, n_items) as i:
                vi = item_variant(pe, i)
                vn = item_variant(pe, i + 1)
                h = large_before(pe, i + 2)
                pe.wait_ge(xT_ready, i * 4 + 4)
                pe.wait_ge(sel_ready, i + 2)
                slot_sums()
                for v in VARIANTS:
                    with pe.If(vi == v):
                        N = STEP * v
                        for j in range(KT):
                            if j % 2 == 0:
                                for m in range(2):
                                    pe.wait_ge(w_exp[m][j // 2], i * 16 + 16)
                            if j >= 3:
                                pe.wait_ge(gu_evac, i * KT + (j - 2))
                            for m in range(2):
                                for k in range(KT):
                                    last = T.matmul(ps[:, j % 3, m * BLOCK:m * BLOCK + N],
                                                    wgt[m][:, k, j * P:(j + 1) * P], xT[:, k, 0:N],
                                                    start=k == 0, stop=k == KT - 1)
                            last.then_inc(gu_psum, 1)
                pe.wait_ge(idx_ready, i + 2)
                pe.wait_ge(xg_in[0], i * 16 + 32)
                pe.wait_ge(xg_in[1], h * 16 + 16)

                def waits(q):
                    if q == 0:
                        pe.wait_ge(sig_ready, i * KT + 1)
                    if q == 3:
                        pe.wait_ge(xT_ready, i * 4 + 5)
                    apart(pe)

                for v in VARIANTS:
                    with pe.If(vn == v):
                        transpose_rows(v, waits)
                for v in VARIANTS:
                    with pe.If(vi == v):
                        N = STEP * v
                        for j in range(KT + 1):
                            if j < KT:
                                if j % 2 == 0:
                                    pe.wait_ge(w_exp[2][j // 2], i * 16 + 16)
                                if j >= 2:
                                    pe.wait_ge(yT_ready, i * KT + (j - 1))
                                for k in range(KT):
                                    if j == 0:
                                        pe.wait_ge(h_ready, i * KT + (k + 1))
                                    last = T.matmul(ps[:, 3 + j % 2, 0:N], wgt[2][:, k, j * P:(j + 1) * P],
                                                    hT[:, k, 0:N], start=k == 0, stop=k == KT - 1)
                                last.then_inc(d_psum, 1)
                            if j >= 1:
                                half, o = divmod(j - 1, 4)
                                pe.wait_ge(yT_ready, i * KT + j)
                                if o == 0 and half == 0:
                                    pe.wait_ge(xT_ready, i * 4 + 7)
                                if o == 0 and half == 1:
                                    pe.wait_ge(xT_ready, i * 4 + 8)
                                    pe.wait_ge(yr_ready, i * 2 + 3)
                                apart(pe)
                                for s in range((N + P - 1) // P):
                                    m = min(P, N - s * P)
                                    last = T.transpose(ps[0:m, ((6, 7), (5, 6))[half][s], o * P:(o + 1) * P],
                                                       yT[:, j - 1, s * P:s * P + m], ident[:])
                                if o == 3:
                                    last.then_inc(yr_psum, 1)


_INS = ["x", "c", "ctx", "c_ctx", "w_ada", "b_ada", "g_pre_mix", "g_post_mix", "g_pre_ffn", "g_post_ffn", "w_in",
        "w_out", "hgrn_lb_logits", "hgrn_norm", "pool_w", "pool_scale", "w_router", "b_router", "w_gate", "b_gate",
        "w_up", "b_up", "w_down", "b_down"]


def kernel(**inputs):
    import numpy as _np
    import concourse.bacc as _bacc
    from concourse import mybir as _mybir
    from concourse.bass_utils import run_bass_kernel_spmd as _run

    nc = _bacc.Bacc("TRN2", target_bir_lowering=False, num_devices=1)
    arrays, args = {}, []
    for name in _INS:
        a = _np.ascontiguousarray(inputs[name])
        arrays[f"in_{name}_dram"] = a
        args.append(nc.dram_tensor(f"in_{name}_dram", a.shape, _mybir.dt.from_np(a.dtype), kind="ExternalInput").ap())
    shape = tuple(inputs["x"].shape)
    args.append(nc.dram_tensor("out_0_dram", shape, _mybir.dt.from_np(_np.dtype("float32")),
                               kind="ExternalOutput").ap())
    hybrid_block_kernel(nc, *args)
    r = _run(nc, [arrays], core_ids=[0])
    return r.results[0]["out_0_dram"]
```
